# Optimizing a Trainium2 kernel written in Bass

```python
import jax, jax.numpy as jnp
from jax import lax
import numpy as np

D_MODEL = 1024
BATCH = 1
SEQ = 256
DEPTH = 2

MLA_HEADS = 16
MLA_NOPE_DIM = 64
MLA_ROPE_DIM = 32
MLA_QK_DIM = MLA_NOPE_DIM + MLA_ROPE_DIM
MLA_V_DIM = 64
MLA_Q_RANK = 768
MLA_KV_RANK = 256
ROPE_THETA = 10000.0
Q_BLOCK = 128
LRU_WIDTH = 1024
LRU_BLOCKS = 4
LRU_BLOCK_W = LRU_WIDTH // LRU_BLOCKS
CONV_WIDTH = 4
LRU_C = 8.0
SWA_HEADS = 16
SWA_KV_HEADS = 2
SWA_GROUP = SWA_HEADS // SWA_KV_HEADS
SWA_HEAD_DIM = 64
WINDOW = 128
N_BRANCH = 3
D_FF = 4 * D_MODEL
EPS = 1e-6

IN_SIZES = (MLA_Q_RANK, MLA_KV_RANK, MLA_ROPE_DIM, LRU_WIDTH, LRU_WIDTH,
            SWA_HEADS * SWA_HEAD_DIM, SWA_KV_HEADS * SWA_HEAD_DIM, SWA_KV_HEADS * SWA_HEAD_DIM,
            N_BRANCH * D_MODEL)
D_IN = sum(IN_SIZES)

kernel_name = "hybrid_mla_rglru_swa_gated_block"

def _split_points():
    pts, acc = [], 0
    for size in IN_SIZES[:-1]:
        acc += size
        pts.append(acc)
    return pts

def rms_norm(x, gain):
    xf = x.astype(jnp.float32)
    y = xf * lax.rsqrt(jnp.mean(jnp.square(xf), axis=-1, keepdims=True) + EPS)
    return (y * gain.astype(jnp.float32)).astype(x.dtype)

def rope_tables(seq):
    pos = jnp.arange(seq, dtype=jnp.float32)
    inv = ROPE_THETA ** (-jnp.arange(0, MLA_ROPE_DIM, 2, dtype=jnp.float32) / MLA_ROPE_DIM)
    ang = pos[:, None] * inv[None, :]
    return jnp.cos(ang), jnp.sin(ang)

def apply_rope(x, cos, sin):
    xf = x.astype(jnp.float32)
    x1, x2 = jnp.split(xf, 2, axis=-1)
    c = cos[None, :, None, :]
    s = sin[None, :, None, :]
    return jnp.concatenate([x1 * c - x2 * s, x2 * c + x1 * s], axis=-1).astype(x.dtype)

def causal_block_attention(q, k, v, scale):
    B, S, H, dq = q.shape
    dv = v.shape[-1]
    nb = S // Q_BLOCK
    qb = q.reshape(B, nb, Q_BLOCK, H, dq).swapaxes(0, 1)
    starts = jnp.arange(nb) * Q_BLOCK
    k_pos = jnp.arange(S)

    def one_block(args):
        q_blk, start = args
        s = jnp.einsum('bqhd,bkhd->bhqk', q_blk, k).astype(jnp.float32) * scale
        mask = k_pos[None, :] <= (start + jnp.arange(Q_BLOCK))[:, None]
        p = jax.nn.softmax(jnp.where(mask, s, -jnp.inf), axis=-1)
        return jnp.einsum('bhqk,bkhd->bqhd', p.astype(v.dtype), v)

    out = lax.map(one_block, (qb, starts))
    return out.swapaxes(0, 1).reshape(B, S, H * dv)

def mla_branch(c_q, c_kv, k_rope, q_a_norm, kv_a_norm, w_uq, w_ukv, q_norm, k_norm, cos, sin):
    B, S, _ = c_q.shape
    q = (rms_norm(c_q, q_a_norm) @ w_uq).reshape(B, S, MLA_HEADS, MLA_QK_DIM)
    kv = (rms_norm(c_kv, kv_a_norm) @ w_ukv).reshape(B, S, MLA_HEADS, MLA_NOPE_DIM + MLA_V_DIM)
    k_nope, v = kv[..., :MLA_NOPE_DIM], kv[..., MLA_NOPE_DIM:]
    q_nope = rms_norm(q[..., :MLA_NOPE_DIM], q_norm[:MLA_NOPE_DIM])
    q_pe = apply_rope(rms_norm(q[..., MLA_NOPE_DIM:], q_norm[MLA_NOPE_DIM:]), cos, sin)
    k_nope = rms_norm(k_nope, k_norm[:MLA_NOPE_DIM])
    k_pe = apply_rope(rms_norm(k_rope, k_norm[MLA_NOPE_DIM:])[:, :, None, :], cos, sin)
    q = jnp.concatenate([q_nope, q_pe], axis=-1)
    k = jnp.concatenate([k_nope, jnp.broadcast_to(k_pe, (B, S, MLA_HEADS, MLA_ROPE_DIM))], axis=-1)
    return causal_block_attention(q, k, v, MLA_QK_DIM ** -0.5)

def block_diag_linear(x, w, b):
    B, S, _ = x.shape
    xb = x.reshape(B, S, LRU_BLOCKS, LRU_BLOCK_W)
    return jnp.einsum('bsnd,nde->bsne', xb, w).reshape(B, S, LRU_WIDTH) + b

def rglru_branch(xr, gate, conv_w, conv_b, w_rg_a, b_rg_a, w_rg_x, b_rg_x, lru_lambda):
    xc = lax.conv_general_dilated(
        xr, conv_w[:, None, :].astype(xr.dtype), window_strides=(1,),
        padding=[(CONV_WIDTH - 1, 0)], dimension_numbers=('NWC', 'WIO', 'NWC'),
        feature_group_count=LRU_WIDTH) + conv_b
    r = jax.nn.sigmoid(block_diag_linear(xc, w_rg_a, b_rg_a).astype(jnp.float32))
    i = jax.nn.sigmoid(block_diag_linear(xc, w_rg_x, b_rg_x).astype(jnp.float32))
    log_a = -LRU_C * r * jax.nn.softplus(-lru_lambda.astype(jnp.float32))
    a = jnp.exp(log_a)
    b = jnp.sqrt(-jnp.expm1(2.0 * log_a)) * (i * xc.astype(jnp.float32))

    def combine(c1, c2):
        a1, b1 = c1
        a2, b2 = c2
        return a1 * a2, a2 * b1 + b2

    _, h = lax.associative_scan(combine, (a, b), axis=1)
    return (h * jax.nn.gelu(gate.astype(jnp.float32))).astype(xr.dtype)

def swa_branch(q, k, v, q_norm, k_norm, sinks):
    B, S, _ = q.shape
    nb = S // WINDOW
    q = rms_norm(q.reshape(B, S, SWA_HEADS, SWA_HEAD_DIM), q_norm)
    k = rms_norm(k.reshape(B, S, SWA_KV_HEADS, SWA_HEAD_DIM), k_norm)
    v = v.reshape(B, S, SWA_KV_HEADS, SWA_HEAD_DIM)
    qb = q.reshape(B, nb, WINDOW, SWA_KV_HEADS, SWA_GROUP, SWA_HEAD_DIM)
    kb = k.reshape(B, nb, WINDOW, SWA_KV_HEADS, SWA_HEAD_DIM)
    vb = v.reshape(B, nb, WINDOW, SWA_KV_HEADS, SWA_HEAD_DIM)
    kk = jnp.concatenate([jnp.concatenate([jnp.zeros_like(kb[:, :1]), kb[:, :-1]], axis=1), kb], axis=2)
    vv = jnp.concatenate([jnp.concatenate([jnp.zeros_like(vb[:, :1]), vb[:, :-1]], axis=1), vb], axis=2)
    s = jnp.einsum('bnqkgd,bnjkd->bnkgqj', qb, kk).astype(jnp.float32) * (SWA_HEAD_DIM ** -0.5)
    qi = jnp.arange(WINDOW)[:, None]
    kj = jnp.arange(2 * WINDOW)[None, :]
    delta = qi + WINDOW - kj
    band = (delta >= 0) & (delta < WINDOW)
    valid = band[None] & ((jnp.arange(nb)[:, None, None] > 0) | (kj[None] >= WINDOW))
    s = jnp.where(valid[None, :, None, None], s, -jnp.inf)
    sink = sinks.astype(jnp.float32).reshape(1, 1, SWA_KV_HEADS, SWA_GROUP, 1, 1)
    m = jnp.maximum(jnp.max(s, axis=-1, keepdims=True), sink)
    p = jnp.exp(s - m)
    attn = p / (jnp.sum(p, axis=-1, keepdims=True) + jnp.exp(sink - m))
    out = jnp.einsum('bnkgqj,bnjkd->bnqkgd', attn.astype(vv.dtype), vv)
    return out.reshape(B, S, SWA_HEADS * SWA_HEAD_DIM)

def hybrid_layer(x, cos, sin, norm1, w_in, mla_q_a_norm, mla_kv_a_norm, w_uq, w_ukv, mla_q_norm,
                 mla_k_norm, conv_w, conv_b, w_rg_a, b_rg_a, w_rg_x, b_rg_x, lru_lambda,
                 swa_q_norm, swa_k_norm, swa_sinks, w_branch, w_out, norm2, w_ff1, w_ff2):
    B, S, D = x.shape
    u = rms_norm(x, norm1) @ w_in
    c_q, c_kv, k_rope, lru_x, lru_gate, sq, sk, sv, gate_logits = jnp.split(u, _split_points(), axis=-1)
    o_a = mla_branch(c_q, c_kv, k_rope, mla_q_a_norm, mla_kv_a_norm, w_uq, w_ukv,
                     mla_q_norm, mla_k_norm, cos, sin)
    o_b = rglru_branch(lru_x, lru_gate, conv_w, conv_b, w_rg_a, b_rg_a, w_rg_x, b_rg_x, lru_lambda)
    o_c = swa_branch(sq, sk, sv, swa_q_norm, swa_k_norm, swa_sinks)
    o = jnp.stack([o_a, o_b, o_c], axis=2)
    branch = jnp.einsum('bsnc,ncd->bsnd', o, w_branch)
    g = jax.nn.sigmoid(gate_logits.astype(jnp.float32)).reshape(B, S, N_BRANCH, D).astype(x.dtype)
    x = x + jnp.sum(g * branch, axis=2) @ w_out
    h = rms_norm(x, norm2)
    return x + jnp.square(jax.nn.relu(h @ w_ff1)) @ w_ff2

def setup_inputs(seed: int = 0) -> dict:
    key = jax.random.key(seed)
    ks = jax.random.split(key, 24)

    def nrm(k, shape, scale):
        return jax.random.normal(k, shape, jnp.float32) * scale

    def gain(k, shape):
        return 1.0 + 0.02 * jax.random.normal(k, shape, jnp.float32)

    u = jax.random.uniform(ks[14], (DEPTH, LRU_WIDTH), jnp.float32, minval=0.9, maxval=0.999)
    s = u ** (1.0 / LRU_C)
    lru_lambda = jnp.log(s) - jnp.log1p(-s)
    return {
        "x": nrm(ks[0], (BATCH, SEQ, D_MODEL), 1.0),
        "norm1": gain(ks[1], (DEPTH, D_MODEL)),
        "w_in": nrm(ks[2], (DEPTH, D_MODEL, D_IN), D_MODEL ** -0.5),
        "mla_q_a_norm": gain(ks[3], (DEPTH, MLA_Q_RANK)),
        "mla_kv_a_norm": gain(ks[4], (DEPTH, MLA_KV_RANK)),
        "w_uq": nrm(ks[5], (DEPTH, MLA_Q_RANK, MLA_HEADS * MLA_QK_DIM), MLA_Q_RANK ** -0.5),
        "w_ukv": nrm(ks[6], (DEPTH, MLA_KV_RANK, MLA_HEADS * (MLA_NOPE_DIM + MLA_V_DIM)), MLA_KV_RANK ** -0.5),
        "mla_q_norm": gain(ks[7], (DEPTH, MLA_QK_DIM)),
        "mla_k_norm": gain(ks[8], (DEPTH, MLA_QK_DIM)),
        "conv_w": nrm(ks[9], (DEPTH, CONV_WIDTH, LRU_WIDTH), CONV_WIDTH ** -0.5),
        "conv_b": nrm(ks[10], (DEPTH, LRU_WIDTH), 0.02),
        "w_rg_a": nrm(ks[11], (DEPTH, LRU_BLOCKS, LRU_BLOCK_W, LRU_BLOCK_W), LRU_BLOCK_W ** -0.5),
        "b_rg_a": nrm(ks[12], (DEPTH, LRU_WIDTH), 0.1),
        "w_rg_x": nrm(ks[13], (DEPTH, LRU_BLOCKS, LRU_BLOCK_W, LRU_BLOCK_W), LRU_BLOCK_W ** -0.5),
        "b_rg_x": nrm(ks[15], (DEPTH, LRU_WIDTH), 0.1),
        "lru_lambda": lru_lambda,
        "swa_q_norm": gain(ks[16], (DEPTH, SWA_HEAD_DIM)),
        "swa_k_norm": gain(ks[17], (DEPTH, SWA_HEAD_DIM)),
        "swa_sinks": nrm(ks[18], (DEPTH, SWA_HEADS), 0.5),
        "w_branch": nrm(ks[19], (DEPTH, N_BRANCH, D_MODEL, D_MODEL), D_MODEL ** -0.5),
        "w_out": nrm(ks[20], (DEPTH, D_MODEL, D_MODEL), D_MODEL ** -0.5),
        "norm2": gain(ks[21], (DEPTH, D_MODEL)),
        "w_ff1": nrm(ks[22], (DEPTH, D_MODEL, D_FF), D_MODEL ** -0.5),
        "w_ff2": nrm(ks[23], (DEPTH, D_FF, D_MODEL), D_FF ** -0.5),
    }

def reference(x, norm1, w_in, mla_q_a_norm, mla_kv_a_norm, w_uq, w_ukv, mla_q_norm, mla_k_norm,
              conv_w, conv_b, w_rg_a, b_rg_a, w_rg_x, b_rg_x, lru_lambda, swa_q_norm, swa_k_norm,
              swa_sinks, w_branch, w_out, norm2, w_ff1, w_ff2):
    cos, sin = rope_tables(x.shape[1])
    for l in range(DEPTH):
        x = hybrid_layer(x, cos, sin, norm1[l], w_in[l], mla_q_a_norm[l], mla_kv_a_norm[l], w_uq[l],
                         w_ukv[l], mla_q_norm[l], mla_k_norm[l], conv_w[l], conv_b[l], w_rg_a[l],
                         b_rg_a[l], w_rg_x[l], b_rg_x[l], lru_lambda[l], swa_q_norm[l], swa_k_norm[l],
                         swa_sinks[l], w_branch[l], w_out[l], norm2[l], w_ff1[l], w_ff2[l])
    return x


_drawn_inputs = setup_inputs


def setup_inputs(seed=0):
    import zlib

    import numpy as np

    out = dict(_drawn_inputs(seed))
    spreads = {}
    factors = {'norm1': 4.133,
     'mla_q_a_norm': 8.0,
     'mla_kv_a_norm': 8.0,
     'mla_q_norm': 8.0,
     'mla_k_norm': 8.0,
     'b_rg_a': 8.0,
     'b_rg_x': 3.054,
     'swa_q_norm': 8.0,
     'swa_k_norm': 8.0,
     'swa_sinks': 19.785,
     'norm2': 2.884}
    for name, (base, spread) in spreads.items():
        noise = np.random.default_rng([zlib.crc32(name.encode()), seed]).standard_normal(out[name].shape)
        drawn = base * np.exp(spread * noise) if base else spread * noise
        out[name] = __import__('jax').numpy.asarray(drawn.astype(out[name].dtype))
    for name, factor in factors.items():
        out[name] = (out[name] * factor).astype(out[name].dtype)
    return out
```

```python
from contextlib import ExitStack

import concourse.bass as bass
from concourse import mybir

F32 = mybir.dt.float32
F32R = mybir.dt.float32r
ACT = mybir.ActivationFunctionType
ALU = mybir.AluOpType
AX = mybir.AxisListType

P = 128
DEPTH = 2
D = 1024
SEQ = 256
DC = D // P
HEADS = 16
NOPE, ROPE = 64, 32
QRANK, KVRANK = 768, 256
EPS = 1e-6
NEG = -1e30
RING = 3
UNIT = 16 * P

U_CQ, U_CKV, U_KK, U_LX, U_SQ, U_SV, U_RA, U_RX, U_LG = 0, 3, 4, 5, 9, 13, 14, 15, 16
U_UQ, U_UK, U_UV, U_GB, U_BB, U_GA, U_GC, U_BA, U_BC = 20, 28, 29, 30, 34, 38, 42, 46, 50
U_OUT, U_FF, UNITS = 54, 58, 90
UQ_COLS, SV_COLS = 12 * P, 8 * P
T_CQ, T_CKV, T_KK, T_LX, T_SQ, T_SV, T_RA, T_RX, T_LG = 0, 3, 4, 5, 9, 13, 14, 18, 22
T_UQ, T_UK, T_UV, T_GB, T_BB, T_GA, T_GC, T_BA, T_BC = 26, 34, 38, 42, 46, 50, 54, 58, 62
T_OUT, FILLS = 66, 70
E_N1, E_CQ, E_KK, E_SQ, E_UQ, E_UK, E_N2, MEANS = 0, 1, 2, 3, 7, 15, 19, 20
FF_J = 16

PARAM_SIZES = (("g1", 8), ("cqg", 6), ("ckvg", 2), ("qge", 1), ("qgo", 1), ("kng", 1), ("krg", 1),
               ("sqg", 1), ("skg", 1), ("cw0", 8), ("cw1", 8), ("cw2", 8), ("cw3", 8), ("cb", 8),
               ("bra", 8), ("brx", 8), ("lam", 8), ("g2", 8), ("sink", 16))
PCOL, NPAR = {}, 0
for _name, _n in PARAM_SIZES:
    PCOL[_name] = NPAR
    NPAR += _n

DVE_CHAIN = 120
ACT_CHAIN = 4


class Signal:

    def __init__(self, sem, per_layer, credit=0):
        self.sem, self.per, self.credit = sem, per_layer, credit

    def at(self, layer, n):
        return layer * self.per + (self.credit + n)


def trunk(nc, x_in, stream, params, cs_tab, mats, masks, out):
    with ExitStack() as ctx:
        def sb(name, shape, dt=F32):
            return ctx.enter_context(nc.sbuf_tensor(name, shape, dt))

        def sig(name, per, credit=0):
            return Signal(ctx.enter_context(nc.semaphore(name)), per, credit)

        raw = sb("raw", [P, RING, UNIT])
        whi = sb("whi", [P, RING, UNIT], F32R)
        wlo = sb("wlo", [P, RING, UNIT], F32R)
        xT = sb("xT", [P, DC, SEQ])
        H_hi, H_lo = sb("H_hi", [P, DC, SEQ], F32R), sb("H_lo", [P, DC, SEQ], F32R)
        Y_hi, Y_lo = sb("Y_hi", [P, DC, SEQ], F32R), sb("Y_lo", [P, DC, SEQ], F32R)
        Z_hi, Z_lo = sb("Z_hi", [P, DC, SEQ], F32R), sb("Z_lo", [P, DC, SEQ], F32R)
        QA = sb("QA", [P, HEADS, SEQ])
        XR = sb("XR", [P, DC, SEQ + 4])
        AB = sb("AB", [P, HEADS, SEQ])
        XC = sb("XC", [P, DC, SEQ])
        SQ = sb("SQ", [P, DC, SEQ])
        KK = sb("KK", [P, 2, SEQ])
        SV = sb("SV", [P, 2, P])
        sq_t = sb("sq_t", [P, 2, 512])
        sd = sb("sd", [P, 2, 512])
        shift = sb("shift", [P, SEQ])
        S = sb("S", [P, 2, 2, 384])
        PT = sb("PT", [P, 2, 2, 384])
        pl = sb("pl", [P, NPAR])
        par = sb("par", [P, DEPTH, NPAR])
        cs = sb("cs", [P, 3, SEQ])
        csg = sb("csg", [P, 2, SEQ])
        mat = sb("mat", [P, 8, P])
        mask = sb("mask", [P, 5 * P])
        zero = sb("zero", [P, P], F32R)
        eps = sb("eps", [P, 1])
        hb = sb("hb", [P, 2, DC])
        sp = sb("sp", [P, DEPTH, DC])
        mark = sb("mark", [P, 4])
        spt = sb("spt", [P, 5, DEPTH * DC])
        nm = sb("nm", [P, 2, 4])
        se = sb("se", [P, 2, 4])
        rs = sb("rs", [P, 2, 4])
        V = XC[:, :, :].rearrange("p c t -> p (c t)").rearrange("p (k n) -> p k n", k=2)
        IDENT, M1024, M768, M256, MEVEN, MODD, M64, M32 = range(8)

        def pc(name, i=0, n=1):
            return pl[:, PCOL[name] + i:PCOL[name] + i + n]

        acc = ctx.enter_context(nc.psum_tensor("acc", [P, 3, 512], F32))
        big = ctx.enter_context(nc.psum_tensor("big", [P, 4, 512], F32))
        po = ctx.enter_context(nc.psum_tensor("po", [P, 512], F32))

        raw_in = [sig(f"raw_in{i}", 16 * UNITS // RING) for i in range(RING)]
        hi_ready = sig("hi_ready", UNITS)
        lo_ready = sig("lo_ready", UNITS)
        unit_used = sig("unit_used", UNITS, RING)
        part_done = sig("part_done", 12)
        evacuated = [sig(f"evacuated{b}", FILLS // 2, 1) for b in range(2)]
        const_in = sig("const_in", 0)
        setup = sig("setup", 0)
        abs_lam = sig("abs_lam", 0)
        x_ready = sig("x_ready", 4, 4)
        x_squared = sig("x_squared", 8)
        mean_done = sig("mean_done", MEANS)
        root_done = sig("root_done", MEANS)
        normed = sig("normed", MEANS, 2)
        xn_ready = sig("xn_ready", 8)
        lat_ready = sig("lat_ready", 4)
        h_hi, h_lo = sig("h_hi", 8), sig("h_lo", 8)
        lat_hi, lat_lo = sig("lat_hi", 4), sig("lat_lo", 4)
        conv_ready = sig("conv_ready", 4)
        xc_hi, xc_lo = sig("xc_hi", 4), sig("xc_lo", 4)
        rope_in = sig("rope_in", 9)
        rope_shifted = sig("rope_shifted", 9)
        roped = sig("roped", 9, 1)
        lru_log = sig("lru_log", 1)
        lru_exp = sig("lru_exp", 2)
        lru_term = sig("lru_term", 1)
        lru_root = sig("lru_root", 1)
        lru_gelu = sig("lru_gelu", 1)
        ob_ready = sig("ob_ready", 4)
        ob_hi, ob_lo = sig("ob_hi", 4), sig("ob_lo", 4)
        k_rows = sig("k_rows", 4)
        scores_done = sig("scores_done", 16)
        masked = sig("masked", 16)
        sink_in = sig("sink_in", 8)
        exped = sig("exped", 16)
        probs_ready = sig("probs_ready", 16, 2)
        turned = sig("turned", 16)
        pt_ready = sig("pt_ready", 16)
        o_done = sig("o_done", 16)
        o_hi, o_lo = sig("o_hi", 16), sig("o_lo", 16)
        sum_ready = sig("sum_ready", 4)
        mg_hi, mg_lo = sig("mg_hi", 4), sig("mg_lo", 4)
        f_square = sig("f_square", FF_J)
        f_relu = sig("f_relu", FF_J)
        f_hi, f_lo = sig("f_hi", FF_J), sig("f_lo", FF_J)
        dve_chain = sig("dve_chain", DVE_CHAIN)
        act_chain = sig("act_chain", ACT_CHAIN)
        out_done = sig("out_done", 0)

        ends = {}
        n_part = 0
        for t0, u0, n, each in ((T_CQ, U_CQ, 14, 1), (T_RA, U_RA, 2, 4), (T_LG, U_LG, 12, 1),
                                (T_UK, U_UK, 2, 4), (T_GB, U_GB, 28, 1)):
            for k in range(n * each):
                if k % each == each - 1:
                    ends[t0 + k] = (unit_used, u0 + k // each + 1)
                else:
                    n_part += 1
                    ends[t0 + k] = (part_done, n_part)

        def filled(l, t):
            s, n = ends[t]
            return s.sem, s.at(l, n)

        def read_out(l, t):
            s = evacuated[t % 2]
            return s.sem, s.at(l, t // 2 + 1)

        block = ctx.enter_context(nc.Block())

        @block.sync
        def _(sp_):
            sp_.dma_start(xT[:, :, :], x_in).then_inc(const_in.sem, 16)
            sp_.dma_start(par[:, :, :], params).then_inc(const_in.sem, 16)
            for s in range(RING):
                sp_.dma_start(raw[:, s, :], stream[s, :, :]).then_inc(raw_in[s].sem, 16)
                if s == 0:
                    sp_.dma_start(mat[:, :, :], mats).then_inc(const_in.sem, 16)
                    sp_.dma_start(cs[:, :, :], cs_tab).then_inc(const_in.sem, 16)
                    sp_.dma_start(mask[:, :], masks).then_inc(const_in.sem, 16)
            with sp_.Fori(0, DEPTH * UNITS // RING - 1) as i:
                for s in range(RING):
                    sp_.wait_ge(lo_ready.sem, i * RING + (s + 1))
                    sp_.dma_start(raw[:, s, :], stream[bass.ds(i * RING + (RING + s), 1), :, :]
                                  .rearrange("a p n -> (a p) n")).then_inc(raw_in[s].sem, 16)
            sp_.wait_ge(x_ready.sem, x_ready.at(DEPTH - 1, 4))
            sp_.dma_start(out, xT[:, :, :]).then_inc(out_done.sem, 16)
            sp_.wait_ge(out_done.sem, 16)

        @block.scalar
        def _(act):
            sc = nc.scalar

            def split_hi(l, u, cols=UNIT, it=0, slot=None):
                s = u % RING if slot is None else slot
                act.wait_ge(raw_in[s].sem, l * raw_in[s].per + it * 32 + 16 * (u // RING + 1))
                act.wait_ge(unit_used.sem, l * UNITS + it * 6 + (u + 1))
                sc.activation(whi[:, s, 0:cols], raw[:, s, 0:cols], ACT.Copy).then_inc(hi_ready.sem, 1)

            def bank(t):
                return acc[:, t % 2, :]

            def two(ap):
                return ap.rearrange("p c t -> p (c t)")

            def evac_copy(l, t, dst, func=ACT.Copy, **kw):
                act.wait_ge(*filled(l, t))
                sc.activation(dst, bank(t), func, **kw).then_inc(evacuated[t % 2].sem, 1)

            def evac_squares(l, t, dst, sq_dst, e=None):
                act.wait_ge(*filled(l, t))
                sc.activation(dst, bank(t), ACT.Copy)
                if e is not None:
                    act.wait_ge(mean_done.sem, mean_done.at(l, e - 1))
                sc.activation(sq_dst, bank(t), ACT.Square).then_inc(evacuated[t % 2].sem, 1)

            def root(l, e, n=512):
                act.wait_ge(mean_done.sem, mean_done.at(l, e + 1))
                act.wait_ge(normed.sem, normed.at(l, e - 1))
                sc.activation(sd[:, e % 2, 0:n], acc[:, 2, 0:n], ACT.Sqrt, bias=eps[:, 0:1])\
                  .then_inc(root_done.sem, 1)

            def hi_pair(l, dst, g, src, ready, n, done, **kw):
                act.wait_ge(ready.sem, ready.at(l, n))
                sc.activation(dst[:, 2 * g:2 * g + 2, :], src, ACT.Copy, **kw).then_inc(done.sem, 1)

            def shift_rows(l, r, lo_src, hi_src):
                act.wait_ge(rope_in.sem, rope_in.at(l, r + 1))
                act.wait_ge(roped.sem, roped.at(l, r))
                sc.activation(shift[32:64, :], lo_src, ACT.Copy)
                sc.activation(shift[64:96, :], hi_src, ACT.Copy).then_inc(rope_shifted.sem, 1)

            def softmax_exp(l, i, kind):
                b = i % 2
                act.wait_ge(masked.sem, masked.at(l, i + 1))
                act.wait_ge(probs_ready.sem, probs_ready.at(l, i - 1))
                for j in range(2):
                    sc.activation(S[:, b, j, 0:128], S[:, b, j, 0:128], ACT.Exp,
                                  bias=nm[:, b, 2 * j:2 * j + 1], accum_out=rs[:, b, 2 * j:2 * j + 1])
                    last = sc.activation(S[:, b, j, 128:384], S[:, b, j, 128:384], ACT.Exp,
                                         bias=nm[:, b, 2 * j + 1:2 * j + 2],
                                         accum_out=rs[:, b, 2 * j + 1:2 * j + 2])
                if kind:
                    act.wait_ge(sink_in.sem, sink_in.at(l, i - 8 + 1))
                    last = sc.activation(se[:, b, :], se[:, b, :], ACT.Exp)
                last.then_inc(exped.sem, 1)

            def turn_out(l, i):
                b = i % 2
                act.wait_ge(turned.sem, turned.at(l, i + 1))
                if i >= 2:
                    act.wait_ge(o_done.sem, o_done.at(l, i - 1))
                sc.activation(PT[:, b, :, :], big[:, 2:4, 0:384], ACT.Copy).then_inc(pt_ready.sem, 1)

            def o_out(l, i):
                act.wait_ge(o_done.sem, o_done.at(l, i + 1))
                dst = (Y_hi if i < 8 else Z_hi)[:, i % 8, :]
                sc.activation(dst, po[:, 0:SEQ], ACT.Copy).then_inc(o_hi.sem, 1)

            act.wait_ge(const_in.sem, 80)
            lam = par[:, :, PCOL["lam"]:PCOL["lam"] + DC]
            sc.activation(spt[:, 0, :].rearrange("p (l c) -> p l c", l=DEPTH), lam, ACT.Abs)\
              .then_inc(abs_lam.sem, 1)
            act.wait_ge(abs_lam.sem, 1)
            sc.activation(spt[:, 1, :], spt[:, 0, :], ACT.Exp, scale=-1.0).then_inc(abs_lam.sem, 1)
            act.wait_ge(setup.sem, 1)

            with act.Fori(0, DEPTH) as l:
                for g in range(4):
                    act.wait_ge(x_ready.sem, x_ready.at(l, g - 3))
                    sc.activation(QA[:, 8 + 2 * g:10 + 2 * g, :], xT[:, 2 * g:2 * g + 2, :], ACT.Square)\
                      .then_inc(x_squared.sem, 1)
                split_hi(l, 0)
                root(l, E_N1, SEQ)
                for g in range(4):
                    hi_pair(l, H_hi, g, XR[:, 2 * g:2 * g + 2, 3:259], xn_ready, g + 1, h_hi)
                    if g == 1:
                        split_hi(l, 1)
                split_hi(l, 2)
                for u in range(1, 5):
                    c = 2 * (u - 1)
                    evac_squares(l, u - 1, two(QA[:, c:c + 2, :]), two(QA[:, 8 + c:10 + c, :]))
                    split_hi(l, u + 2)
                evac_squares(l, T_KK, two(KK[:, :, :]), sq_t[:, E_KK % 2, :], E_KK)
                split_hi(l, 7)
                root(l, E_CQ)
                evac_copy(l, T_LX, XR[:, 0:2, 3:259])
                split_hi(l, 8)
                for g in range(4):
                    hi_pair(l, Y_hi, g, QA[:, 2 * g:2 * g + 2, :], lat_ready, g + 1, lat_hi)
                root(l, E_KK)
                evac_copy(l, T_LX + 1, XR[:, 2:4, 3:259])
                split_hi(l, 9)
                shift_rows(l, 0, KK[0:32, 1, :], KK[96:128, 1, :])
                evac_copy(l, T_LX + 2, XR[:, 4:6, 3:259])
                split_hi(l, 10)
                evac_copy(l, T_LX + 3, XR[:, 6:8, 3:259])
                split_hi(l, 11)
                for g in range(4):
                    evac_squares(l, T_SQ + g, two(SQ[:, 2 * g:2 * g + 2, :]), sq_t[:, (E_SQ + g) % 2, :],
                                 E_SQ + g)
                    split_hi(l, 12 + g, SV_COLS if 12 + g == U_SV else UNIT)
                    if g:
                        root(l, E_SQ + g - 1)
                    hi_pair(l, Z_hi, g, XC[:, 2 * g:2 * g + 2, :], conv_ready, g + 1, xc_hi)
                act.wait_ge(*filled(l, T_SV))
                sc.activation(SV[:, :, :].rearrange("p k n -> p (k n)"), acc[:, T_SV % 2, 0:256], ACT.Copy)\
                  .then_inc(evacuated[T_SV % 2].sem, 1)
                split_hi(l, 16)
                root(l, E_SQ + 3)
                for gate in range(2):
                    if gate:
                        split_hi(l, 17)
                    for g in range(4):
                        t = T_RA + 4 * gate + g
                        act.wait_ge(*filled(l, t))
                        for h in range(2):
                            c = 2 * g + h
                            last = sc.activation(AB[:, 8 * gate + c, :], acc[:, t % 2, h * 256:h * 256 + 256],
                                                 ACT.Tanh, bias=hb[:, gate, c:c + 1], scale=0.5)
                        last.then_inc(evacuated[t % 2].sem, 1)
                split_hi(l, 18)
                act.wait_ge(lru_log.sem, lru_log.at(l, 1))
                ab0 = AB[:, 0:8, :].rearrange("p c t -> p (c t)")
                lterm = QA[:, 8:16, :].rearrange("p c t -> p (c t)")
                sc.activation(lterm, ab0, ACT.Tanh, scale=-1.0).then_inc(lru_exp.sem, 1)
                sc.activation(ab0, ab0, ACT.Exp).then_inc(lru_exp.sem, 1)
                for g in range(4):
                    evac_copy(l, T_LG + g, XR[:, 2 * g:2 * g + 2, 3:259])
                    split_hi(l, 19 + g, UQ_COLS if 19 + g >= U_UQ else UNIT)
                    if g == 0:
                        act.wait_ge(lru_term.sem, lru_term.at(l, 1))
                        sc.activation(lterm, lterm, ACT.Sqrt, scale=0.25).then_inc(lru_root.sem, 1)
                for t in (T_LG + 2, T_LG + 3):
                    act.wait_ge(*read_out(l, t))
                sc.activation(XR[:, :, 3:259], XR[:, :, 3:259], ACT.Gelu_apprx_tanh).then_inc(lru_gelu.sem, 1)
                for g in range(8):
                    u = U_UQ + 1 + g
                    evac_squares(l, T_UQ + g, two(QA[:, 2 * g:2 * g + 2, :]), sq_t[:, (E_UQ + g) % 2, :],
                                 E_UQ + g)
                    split_hi(l, u + 2, UQ_COLS if u + 2 < U_UK else UNIT)
                    if g:
                        root(l, E_UQ + g - 1)
                    if g >= 2:
                        shift_rows(l, g - 1, QA[0:32, 2 * (g - 2) + 1, :], QA[96:128, 2 * (g - 2), :])
                    if g in (3, 4, 5, 6):
                        hi_pair(l, Z_hi, g - 3, XC[:, 2 * (g - 3):2 * (g - 3) + 2, :], ob_ready, g - 2, ob_hi)
                for g in range(4):
                    t, e = T_UK + g, E_UK + g
                    act.wait_ge(*filled(l, t))
                    for h in range(2):
                        p0 = 64 * h
                        sc.activation(AB[p0:p0 + 64, 4 * g + h:4 * g + h + 3:2, :],
                                      acc[p0:p0 + 64, t % 2, :].rearrange("p (c t) -> p c t", c=2), ACT.Copy)
                    if g >= 2:
                        root(l, e - 2)
                    act.wait_ge(mean_done.sem, mean_done.at(l, e - 1))
                    sc.activation(sq_t[:, e % 2, :], bank(t), ACT.Square).then_inc(evacuated[t % 2].sem, 1)
                    if g == 0:
                        root(l, E_UQ + 7)
                        shift_rows(l, 7, QA[0:32, 13, :], QA[96:128, 12, :])
                split_hi(l, 31)
                act.wait_ge(ob_lo.sem, ob_lo.at(l, 4))
                for g in range(4):
                    t = T_UV + g
                    act.wait_ge(*filled(l, t))
                    sc.activation(V[:, g // 2, 512 * (g % 2):512 * (g % 2) + 512], bank(t), ACT.Copy)\
                      .then_inc(evacuated[t % 2].sem, 1)
                    if g < 2:
                        root(l, E_UK + 2 + g)
                    if g == 1:
                        shift_rows(l, 8, QA[0:32, 15, :], QA[96:128, 14, :])
                for s in range(18):
                    u = U_GB + s
                    if s >= 1:
                        t = T_GB + s - 1
                        if s <= 4:
                            evac_copy(l, t, XR[:, 2 * s - 2:2 * s, 3:259], ACT.Tanh, scale=0.5)
                        elif 9 <= s <= 16:
                            c = 2 * (s - 9)
                            evac_copy(l, t, two(AB[:, c:c + 2, :]), ACT.Tanh, scale=0.5)
                    if 1 <= s <= 16:
                        turn_out(l, s - 1)
                    split_hi(l, u + 2)
                    if 2 <= s:
                        o_out(l, s - 2)
                    if s < 16:
                        softmax_exp(l, s, s >= 8)
                for u in range(U_GB + 18, U_OUT):
                    split_hi(l, u + 2)
                    if u - U_BC - 1 >= 0:
                        g = u - U_BC - 1
                        hi_pair(l, H_hi, g, XR[:, 2 * g:2 * g + 2, 3:259], sum_ready, g + 1, mg_hi, scale=0.5)
                hi_pair(l, H_hi, 3, XR[:, 6:8, 3:259], sum_ready, 4, mg_hi, scale=0.5)
                for u in range(U_OUT, U_OUT + 4):
                    split_hi(l, u + 2)
                    if u > U_OUT:
                        g = u - U_OUT - 1
                        act.wait_ge(*read_out(l, T_OUT + g))
                        sc.activation(QA[:, 8 + 2 * g:10 + 2 * g, :], xT[:, 2 * g:2 * g + 2, :], ACT.Square)\
                          .then_inc(x_squared.sem, 1)
                act.wait_ge(*read_out(l, T_OUT + 3))
                sc.activation(QA[:, 14:16, :], xT[:, 6:8, :], ACT.Square).then_inc(x_squared.sem, 1)
                root(l, E_N2, SEQ)
                for g in range(4):
                    hi_pair(l, Y_hi, g, XR[:, 2 * g:2 * g + 2, 3:259], xn_ready, 5 + g, h_hi)

                def relu_pair(j, it=0):
                    slot, u = j % 3, U_FF if j == 0 else U_FF - 1 + 2 * j
                    act.wait_ge(unit_used.sem, l * UNITS + it * 6 + (RING + u + 1))
                    sc.activation(two(QA[:, 2 * slot:2 * slot + 2, :]), acc[:, slot, :], ACT.Relu)\
                      .then_inc(f_relu.sem, 1)
                    act.wait_ge(f_relu.sem, l * FF_J + it * 3 + (j + 1))
                    sc.activation(H_hi[:, 2 * slot:2 * slot + 2, :], QA[:, 2 * slot:2 * slot + 2, :],
                                  ACT.Square).then_inc(f_hi.sem, 1)

                split_hi(l, U_FF + 2)
                relu_pair(0)
                split_hi(l, U_FF + 3)
                with act.Fori(0, 4) as it:
                    for j in range(1, 4):
                        relu_pair(j, it)
                        split_hi(l, U_FF + 2 + 2 * j, it=it)
                        split_hi(l, U_FF + 3 + 2 * j, it=it)
                for j in range(13, FF_J):
                    relu_pair(j)
                    if j < FF_J - 1:
                        split_hi(l, U_FF + 2 + 2 * j)
                        split_hi(l, U_FF + 3 + 2 * j)

        @block.vector
        def _(dve):
            v = nc.vector
            n_chain = [0]

            def link(ins):
                n_chain[0] += 1
                return ins.then_inc(dve_chain.sem, 1)

            def split_lo(l, u, cols=UNIT, it=0):
                s = u % RING
                dve.wait_ge(hi_ready.sem, l * UNITS + it * 6 + (u + 1))
                v.tensor_tensor(wlo[:, s, 0:cols], raw[:, s, 0:cols], whi[:, s, 0:cols].bitcast(F32),
                                ALU.subtract).then_inc(lo_ready.sem, 1)

            def lo_pair(l, lo, hi, g, src, ready, n, done):
                dve.wait_ge(ready.sem, ready.at(l, n))
                v.tensor_tensor(lo[:, 2 * g:2 * g + 2, :], src, hi[:, 2 * g:2 * g + 2, :].bitcast(F32),
                                ALU.subtract).then_inc(done.sem, 1)

            dve.wait_ge(const_in.sem, 80)
            v.memset(XR[:, :, :], 0.0)
            v.memset(zero[:, :].bitcast(F32), 0.0)
            v.memset(eps[:, :], EPS)
            pre = sig("pre_chain", 0)
            n_pre = [0]

            def pre_link(ins):
                n_pre[0] += 1
                ins.then_inc(pre.sem, 1)
                dve.wait_ge(pre.sem, n_pre[0])

            e_, r_, z_, z2, s_ = (spt[:, k, :] for k in (1, 2, 2, 3, 4))
            dve.wait_ge(abs_lam.sem, 2)
            pre_link(v.tensor_scalar(r_, e_, 2.0, None, ALU.add))
            pre_link(v.reciprocal(r_, r_))
            pre_link(v.tensor_tensor(z_, e_, r_, ALU.mult))
            pre_link(v.tensor_tensor(z2, z_, z_, ALU.mult))
            pre_link(v.tensor_scalar(s_, z2, 1.0 / 19.0, None, ALU.mult))
            for k in range(17, 1, -2):
                pre_link(v.scalar_tensor_tensor(s_, s_, 1.0 / k, z2, ALU.add, ALU.mult))
            pre_link(v.scalar_tensor_tensor(s_, s_, 1.0, z_, ALU.add, ALU.mult))
            lam = par[:, :, PCOL["lam"]:PCOL["lam"] + DC]
            neg = spt[:, 0, :].rearrange("p (l c) -> p l c", l=DEPTH)
            pre_link(v.tensor_scalar(neg, lam, -1.0, 0.0, ALU.mult, ALU.max))
            pre_link(v.scalar_tensor_tensor(s_, s_, 2.0, spt[:, 0, :], ALU.mult, ALU.add))
            pre_link(v.tensor_scalar(sp[:, :, :].rearrange("p l c -> p (l c)"), s_, -4.0, None, ALU.mult))
            dve.sem_inc(unit_used.sem, RING)
            dve.sem_inc(evacuated[0].sem, 1)
            dve.sem_inc(evacuated[1].sem, 1)
            dve.sem_inc(x_ready.sem, 4)
            dve.sem_inc(normed.sem, 2)
            dve.sem_inc(roped.sem, 1)
            dve.sem_inc(probs_ready.sem, 2)
            v.memset(rs[:, :, :], 0.0).then_inc(setup.sem, 1)

            with dve.Fori(0, DEPTH) as l:
                n_chain[0] = 0

                def linked():
                    dve.wait_ge(dve_chain.sem, dve_chain.at(l, n_chain[0]))

                def inverse(e, n=512):
                    dve.wait_ge(root_done.sem, root_done.at(l, e + 1))
                    link(v.reciprocal(sd[:, e % 2, 0:n], sd[:, e % 2, 0:n]))
                    linked()

                def norm_x(e, gain, n0):
                    hi, lo = (H_hi, H_lo) if n0 == 0 else (Y_hi, Y_lo)
                    inverse(e, SEQ)
                    for g in range(5):
                        if g < 4:
                            for c in (2 * g, 2 * g + 1):
                                last = v.scalar_tensor_tensor(XR[:, c, 3:259], xT[:, c, :], pc(gain, c),
                                                              sd[:, e % 2, 0:SEQ], ALU.mult, ALU.mult)
                            last.then_inc(xn_ready.sem, 1)
                        if g:
                            lo_pair(l, lo, hi, g - 1, XR[:, 2 * g - 2:2 * g, 3:259], h_hi, n0 + g, h_lo)
                    v.memset(mark[:, n0 // 4:n0 // 4 + 1], 0.0).then_inc(normed.sem, 1)

                def norm_pair(e, dst, gain):
                    inverse(e)
                    v.scalar_tensor_tensor(dst, dst, gain, sd[:, e % 2, :], ALU.mult, ALU.mult)\
                     .then_inc(normed.sem, 1)

                def conv(g):
                    dve.wait_ge(*read_out(l, T_LX + g))
                    for c in (2 * g, 2 * g + 1):
                        last = link(v.tensor_scalar(XC[:, c, :], XR[:, c, 3:259], pc("cw3", c), pc("cb", c),
                                                    ALU.mult, ALU.add))
                    for k in (2, 1, 0):
                        linked()
                        for c in (2 * g, 2 * g + 1):
                            last = v.scalar_tensor_tensor(XC[:, c, :], XR[:, c, k:k + SEQ],
                                                          pc(f"cw{k}", c), XC[:, c, :], ALU.mult, ALU.add)
                            if k:
                                link(last)
                    last.then_inc(conv_ready.sem, 1)

                def rope_add(r, rows):
                    dve.wait_ge(rope_shifted.sem, rope_shifted.at(l, r + 1))
                    for p0, dst in rows:
                        last = v.tensor_tensor(dst, dst, shift[p0:p0 + 32, :], ALU.add)
                    last.then_inc(roped.sem, 1)

                def q_rope(g):
                    rope_add(g + 1, ((64, QA[64:96, 2 * g, :]), (32, QA[32:64, 2 * g + 1, :])))

                link(v.tensor_copy(pl[:, :], par[:, bass.ds(l, 1), :].rearrange("p a n -> p (a n)")))
                linked()
                v.tensor_scalar(hb[:, 0, :], pc("bra", 0, 8), 0.5, None, ALU.mult)
                v.tensor_scalar(hb[:, 1, :], pc("brx", 0, 8), 0.5, None, ALU.mult)
                link(v.tensor_copy(spt[:, 0, 0:DC], sp[:, bass.ds(l, 1), :].rearrange("p a n -> p (a n)")))
                split_lo(l, 0)
                norm_x(E_N1, "g1", 0)
                split_lo(l, 1)
                split_lo(l, 2)
                qk_scale = float(NOPE + ROPE) ** -0.5
                v.tensor_scalar(csg[:, 0, :], cs[:, 0, :], pc("qge"), qk_scale, ALU.mult, ALU.mult)
                link(v.tensor_scalar(csg[:, 1, :], cs[:, 1, :], pc("qgo"), qk_scale, ALU.mult, ALU.mult))
                link(v.tensor_scalar(pc("sqg"), pc("sqg"), 0.125, None, ALU.mult))
                for u in range(1, 5):
                    split_lo(l, u + 2)
                split_lo(l, 7)
                inverse(E_CQ)
                for c in range(8):
                    half = c // 6
                    last = v.scalar_tensor_tensor(QA[:, c, :], QA[:, c, :], pc("cqg", c),
                                                  sd[:, E_CQ % 2, 256 * half:256 * half + 256],
                                                  ALU.mult, ALU.mult)
                    if c % 2:
                        last.then_inc(lat_ready.sem, 1)
                v.memset(mark[:, 3:4], 0.0).then_inc(normed.sem, 1)
                split_lo(l, 8)
                for g in range(4):
                    lo_pair(l, Y_lo, Y_hi, g, QA[:, 2 * g:2 * g + 2, :], lat_hi, g + 1, lat_lo)
                inverse(E_KK)
                v.scalar_tensor_tensor(KK[:, 0, :], KK[:, 0, :], pc("skg"), sd[:, E_KK % 2, 0:SEQ],
                                       ALU.mult, ALU.mult)
                link(v.scalar_tensor_tensor(KK[:, 1, :], KK[:, 1, :], pc("krg"), sd[:, E_KK % 2, SEQ:512],
                                            ALU.mult, ALU.mult))
                n_kk = n_chain[0]
                split_lo(l, 9)
                dve.wait_ge(dve_chain.sem, dve_chain.at(l, n_kk))
                v.tensor_tensor(KK[:, 1, :], KK[:, 1, :], cs[:, 2, :], ALU.mult).then_inc(rope_in.sem, 1)
                v.memset(mark[:, 2:3], 0.0).then_inc(normed.sem, 1)
                conv(0)
                rope_add(0, ((64, KK[64:96, 1, :]), (32, KK[32:64, 1, :])))
                for g in range(1, 4):
                    split_lo(l, 9 + g)
                    conv(g)
                for g in range(4):
                    split_lo(l, 13 + g, SV_COLS if 13 + g == U_SV else UNIT)
                    lo_pair(l, Z_lo, Z_hi, g, XC[:, 2 * g:2 * g + 2, :], xc_hi, g + 1, xc_lo)
                    norm_pair(E_SQ + g, SQ[:, 2 * g:2 * g + 2, :].rearrange("p c t -> p (c t)"), pc("sqg"))
                split_lo(l, 17)
                dve.wait_ge(*read_out(l, T_RA + 3))
                dve.wait_ge(*read_out(l, T_RA + 2))
                linked()
                v.scalar_tensor_tensor(AB[:, 0:8, :], AB[:, 0:8, :], 1.0,
                                       spt[:, 0, 0:DC].unsqueeze(2).to_broadcast([P, DC, SEQ]),
                                       ALU.add, ALU.mult).then_inc(lru_log.sem, 1)
                split_lo(l, 18)
                dve.wait_ge(*read_out(l, T_RX + 3))
                dve.wait_ge(*read_out(l, T_RX + 2))
                link(v.scalar_tensor_tensor(AB[:, 8:16, :], AB[:, 8:16, :], 1.0, XC[:, :, :],
                                            ALU.add, ALU.mult))
                dve.wait_ge(lru_exp.sem, lru_exp.at(l, 2))
                link(v.tensor_tensor(QA[:, 0:8, :], AB[:, 0:8, :], AB[:, 0:8, :], ALU.mult))
                linked()
                v.scalar_tensor_tensor(QA[:, 8:16, :], QA[:, 0:8, :], 1.0, QA[:, 8:16, :],
                                       ALU.add, ALU.mult).then_inc(lru_term.sem, 1)
                split_lo(l, 19)
                split_lo(l, 20, UQ_COLS)
                dve.wait_ge(lru_root.sem, lru_root.at(l, 1))
                link(v.tensor_tensor(AB[:, 8:16, :], AB[:, 8:16, :], QA[:, 8:16, :], ALU.mult))
                split_lo(l, 21, UQ_COLS)
                linked()
                for c in range(DC):
                    last = link(v.tensor_tensor_scan(XC[:, c, :], AB[:, c, :], AB[:, 8 + c, :], 0.0,
                                                     ALU.mult, ALU.add))
                split_lo(l, 22, UQ_COLS)
                dve.wait_ge(lru_gelu.sem, lru_gelu.at(l, 1))
                linked()
                for g in range(4):
                    v.tensor_tensor(XC[:, 2 * g:2 * g + 2, :], XC[:, 2 * g:2 * g + 2, :],
                                    XR[:, 2 * g:2 * g + 2, 3:259], ALU.mult).then_inc(ob_ready.sem, 1)

                def q_pair(g):
                    e = E_UQ + g
                    inverse(e)
                    qf = QA[:, 2 * g:2 * g + 2, :].rearrange("p c t -> p (c t)")
                    v.tensor_tensor(qf, qf, sd[:, e % 2, :], ALU.mult).then_inc(normed.sem, 1)
                    dve.wait_ge(normed.sem, normed.at(l, e + 1))
                    v.tensor_tensor(QA[:, 2 * g:2 * g + 2, :], QA[:, 2 * g:2 * g + 2, :], csg[:, :, :],
                                    ALU.mult).then_inc(rope_in.sem, 1)

                for g in range(8):
                    u = U_UQ + 1 + g
                    split_lo(l, u + 2, UQ_COLS if u + 2 < U_UK else UNIT)
                    if g >= 1:
                        q_pair(g - 1)
                    if g >= 2:
                        q_rope(g - 2)
                    if g in (4, 5, 6, 7):
                        lo_pair(l, Z_lo, Z_hi, g - 4, XC[:, 2 * (g - 4):2 * (g - 4) + 2, :], ob_hi, g - 3,
                                ob_lo)
                q_pair(7)
                q_rope(6)
                for g in range(4):
                    e = E_UK + g
                    inverse(e)
                    if g == 2:
                        split_lo(l, 31)
                    for h in range(2):
                        p0 = 64 * h
                        kd = AB[p0:p0 + 64, 4 * g + h:4 * g + h + 3:2, :]
                        last = v.scalar_tensor_tensor(
                            kd, kd, pc("kng")[p0:p0 + 64, :],
                            sd[p0:p0 + 64, e % 2, :].rearrange("p (c t) -> p c t", c=2), ALU.mult, ALU.mult)
                    last.then_inc(normed.sem, 1)
                q_rope(7)

                def mask_max(i, kind):
                    b = i % 2
                    dve.wait_ge(scores_done.sem, scores_done.at(l, i + 1))
                    if i >= 2:
                        dve.wait_ge(turned.sem, turned.at(l, i - 1))
                    link(v.tensor_tensor(S[:, b, :, :], big[:, 0:2, 0:384],
                                         mask[:, 256 * (1 - kind):256 * (1 - kind) + 384].unsqueeze(1).to_broadcast([P, 2, 384]), ALU.add))
                    linked()
                    nm2 = nm[:, b, :].rearrange("p (h t) -> p h t", h=2)
                    last = v.tensor_reduce(nm2[:, :, 0], S[:, b, :, 0:128], axis=AX.X, op=ALU.max, negate=True)
                    if kind:
                        link(last)
                    last = v.tensor_reduce(nm2[:, :, 1], S[:, b, :, 128:384], axis=AX.X, op=ALU.max,
                                           negate=True)
                    if not kind:
                        last.then_inc(masked.sem, 1)
                        return
                    link(last)
                    linked()
                    sk = pl[:, PCOL["sink"] + i - 8:PCOL["sink"] + i - 8 + 9:8].unsqueeze(2)\
                        .to_broadcast([P, 2, 2])
                    v.scalar_tensor_tensor(nm2, sk, -1.0, nm2, ALU.mult, ALU.min).then_inc(masked.sem, 1)
                    dve.wait_ge(masked.sem, masked.at(l, i + 1))
                    v.tensor_tensor(se[:, b, :].rearrange("p (h t) -> p h t", h=2), nm2, sk, ALU.add)\
                     .then_inc(sink_in.sem, 1)

                def normalise(i, kind):
                    b = i % 2
                    dve.wait_ge(exped.sem, exped.at(l, i + 1))
                    if kind:
                        link(v.tensor_tensor(rs[:, b, :], rs[:, b, :], se[:, b, :], ALU.add))
                        linked()
                    link(v.reciprocal(rs[:, b, :], rs[:, b, :]))
                    linked()
                    rs2 = rs[:, b, :].rearrange("p (h t) -> p h t", h=2)
                    v.tensor_tensor(S[:, b, :, 0:128], S[:, b, :, 0:128],
                                    rs2[:, :, 0:1].to_broadcast([P, 2, 128]), ALU.mult)
                    v.tensor_tensor(S[:, b, :, 128:384], S[:, b, :, 128:384],
                                    rs2[:, :, 1:2].to_broadcast([P, 2, 256]), ALU.mult)\
                     .then_inc(probs_ready.sem, 1)

                def o_rest(i):
                    dve.wait_ge(o_hi.sem, o_hi.at(l, i + 1))
                    hi, lo = (Y_hi, Y_lo) if i < 8 else (Z_hi, Z_lo)
                    v.tensor_tensor(lo[:, i % 8, :], po[:, 0:SEQ], hi[:, i % 8, :].bitcast(F32),
                                    ALU.subtract).then_inc(o_lo.sem, 1)

                def gate_mul(dst, th, t):
                    dve.wait_ge(*filled(l, t))
                    return v.scalar_tensor_tensor(dst, th, 1.0, acc[:, t % 2, :].rearrange(
                        "p (c t) -> p c t", c=2), ALU.add, ALU.mult)

                for s in range(18):
                    u = U_GB + s
                    if s < 16:
                        mask_max(s, int(s >= 8))
                    if 5 <= s <= 8:
                        t = T_GB + s - 1
                        c = 2 * (s - 5)
                        dve.wait_ge(*read_out(l, T_GB + s - 5))
                        gate_mul(XR[:, c:c + 2, 3:259], XR[:, c:c + 2, 3:259], t)\
                            .then_inc(evacuated[t % 2].sem, 1)
                    if s == 17:
                        t = T_BA
                        dve.wait_ge(*read_out(l, T_GA))
                        dve.wait_ge(*filled(l, t))
                        tm = QA[:, 0:2, :]
                        gate_mul(tm, AB[:, 0:2, :], t).then_inc(evacuated[t % 2].sem, 1)
                        dve.wait_ge(*read_out(l, t))
                        link(v.tensor_tensor(XR[:, 0:2, 3:259], XR[:, 0:2, 3:259], tm, ALU.add))
                    split_lo(l, u + 2)
                    if s >= 2:
                        o_rest(s - 2)
                    if s < 16:
                        normalise(s, int(s >= 8))
                for k in range(1, 8):
                    t, c = T_BA + k, 2 * (k % 4)
                    tm = QA[:, c:c + 2, :]
                    dve.wait_ge(*read_out(l, T_GA + k))
                    gate_mul(tm, AB[:, (0 if k < 4 else 8) + c:(0 if k < 4 else 8) + c + 2, :], t)\
                        .then_inc(evacuated[t % 2].sem, 1)
                    dve.wait_ge(*read_out(l, t))
                    last = v.tensor_tensor(XR[:, c:c + 2, 3:259], XR[:, c:c + 2, 3:259], tm, ALU.add)
                    if k < 4:
                        link(last)
                        if k == 3:
                            linked()
                    else:
                        last.then_inc(sum_ready.sem, 1)
                    split_lo(l, U_BA + k + 3)
                    if k >= 4:
                        dve.wait_ge(mg_hi.sem, mg_hi.at(l, k - 3))
                        v.scalar_tensor_tensor(H_lo[:, c:c + 2, :], XR[:, c:c + 2, 3:259], 0.5,
                                               H_hi[:, c:c + 2, :].bitcast(F32), ALU.mult, ALU.subtract)\
                         .then_inc(mg_lo.sem, 1)
                for g in range(4):
                    t = T_OUT + g
                    if g == 0:
                        split_lo(l, U_OUT + 3)
                    dve.wait_ge(*filled(l, t))
                    v.tensor_tensor(xT[:, 2 * g:2 * g + 2, :], xT[:, 2 * g:2 * g + 2, :],
                                    acc[:, t % 2, :].rearrange("p (c t) -> p c t", c=2), ALU.add)\
                     .then_inc(evacuated[t % 2].sem, 1)
                    if g < 2:
                        split_lo(l, U_OUT + 4 + g)
                norm_x(E_N2, "g2", 4)

                def relu_rest(j, it=0):
                    slot, n = j % 3, l * FF_J + it * 3 + (j + 1)
                    fr, fq = QA[:, 2 * slot:2 * slot + 2, :], QA[:, 6 + 2 * slot:8 + 2 * slot, :]
                    dve.wait_ge(f_relu.sem, n)
                    v.tensor_tensor(fq, fr, fr, ALU.mult).then_inc(f_square.sem, 1)
                    dve.wait_ge(f_square.sem, n)
                    dve.wait_ge(f_hi.sem, n)
                    v.tensor_tensor(H_lo[:, 2 * slot:2 * slot + 2, :], fq,
                                    H_hi[:, 2 * slot:2 * slot + 2, :].bitcast(F32), ALU.subtract)\
                     .then_inc(f_lo.sem, 1)

                split_lo(l, U_FF + 2)
                relu_rest(0)
                split_lo(l, U_FF + 3)
                with dve.Fori(0, 4) as it:
                    for j in range(1, 4):
                        relu_rest(j, it)
                        split_lo(l, U_FF + 2 + 2 * j, it=it)
                        split_lo(l, U_FF + 3 + 2 * j, it=it)
                for j in range(13, FF_J):
                    relu_rest(j)
                    if j < FF_J - 1:
                        split_lo(l, U_FF + 2 + 2 * j)
                        split_lo(l, U_FF + 3 + 2 * j)
                dve.wait_ge(unit_used.sem, unit_used.at(l, UNITS))
                for g in range(4):
                    v.tensor_tensor(xT[:, 2 * g:2 * g + 2, :], xT[:, 2 * g:2 * g + 2, :],
                                    big[:, g, :].rearrange("p (c t) -> p c t", c=2), ALU.add)\
                     .then_inc(x_ready.sem, 1)
                assert n_chain[0] == DVE_CHAIN, n_chain[0]

        @block.gpsimd
        def _(pool):
            for l in range(DEPTH):
                pool.wait_ge(ob_ready.sem, ob_ready.at(l, 4))
                pool.wait_ge(roped.sem, roped.at(l, 1))
                nc.gpsimd.memset(AB[96:128, 0:16:2, :], 0.0).then_inc(k_rows.sem, 1)
                nc.gpsimd.memset(AB[0:32, 1:16:2, :], 0.0).then_inc(k_rows.sem, 1)
                nc.gpsimd.tensor_copy(AB[64:96, 0:16:2, :], KK[64:96, 1:2, :].to_broadcast([32, 8, SEQ]))\
                  .then_inc(k_rows.sem, 1)
                nc.gpsimd.tensor_copy(AB[32:64, 1:16:2, :], KK[32:64, 1:2, :].to_broadcast([32, 8, SEQ]))\
                  .then_inc(k_rows.sem, 1)

        @block.tensor
        def _(pe):
            mm = nc.tensor.matmul

            def product(dst, s, col, hi, lo, first, last, **kw):
                w_hi, w_lo = whi[:, s, col:col + P], wlo[:, s, col:col + P]
                mm(dst, w_hi, hi, start=first, stop=False, **kw)
                mm(dst, w_hi, lo, start=False, stop=False, **kw)
                return mm(dst, w_lo, hi, start=False, stop=last, **kw)

            def pair(l, u, t, op, kc, arrive=None):
                pe.wait_ge(lo_ready.sem, lo_ready.at(l, u + 1))
                pe.wait_ge(*read_out(l, t - 2))
                for h in range(2):
                    for k in range(kc):
                        if arrive and h == 0 and k % 2 == 0:
                            pe.wait_ge(arrive[0].sem, arrive[0].at(l, arrive[1] + k // 2 + 1))
                        last = product(acc[:, t % 2, 256 * h:256 * h + 256], u % RING, (h * kc + k) * P,
                                       op[0][:, k, :], op[1][:, k, :], k == 0, k == kc - 1)
                last.then_inc(unit_used.sem, 1)

            def mean(l, e, half, m, n, last):
                for k, src in enumerate(m):
                    ins = mm(acc[:, 2, 256 * half:256 * half + 256], mat[:, n, :], src,
                             start=(k == 0), stop=(k == len(m) - 1))
                if last:
                    ins.then_inc(mean_done.sem, 1)

            def mean_pair(l, e, t, m0, m1):
                pe.wait_ge(*read_out(l, t))
                pe.wait_ge(root_done.sem, root_done.at(l, e))
                b = e % 2
                mean(l, e, 0, [sq_t[:, b, 0:256]], m0, False)
                mean(l, e, 1, [sq_t[:, b, 256:512]], m1, True)

            def mean_x(l, e, n0):
                for g in range(4):
                    pe.wait_ge(x_squared.sem, x_squared.at(l, n0 + g + 1))
                    for k in (2 * g, 2 * g + 1):
                        ins = mm(acc[:, 2, 0:256], mat[:, M1024, :], QA[:, 8 + k, :], start=(k == 0),
                                 stop=(k == 7))
                ins.then_inc(mean_done.sem, 1)

            def scores(l, i):
                if i < 8:
                    if i == 0:
                        pe.wait_ge(k_rows.sem, k_rows.at(l, 4))
                        pe.wait_ge(normed.sem, normed.at(l, E_UK + 4))
                        pe.wait_ge(roped.sem, roped.at(l, 9))
                if i:
                    pe.wait_ge(masked.sem, masked.at(l, i))
                for j in range(2):
                    if i < 8:
                        q, k = QA[:, 2 * i + j, :], AB[:, 2 * i + j, :]
                    else:
                        q, k = SQ[64 * j:64 * j + 64, i - 8, :], KK[64 * j:64 * j + 64, 0, :]
                    mm(big[:, j, 0:128], q[:, 0:128], k[:, 0:128], start=True, stop=True)
                    last = mm(big[:, j, 128:384], q[:, 128:256], k[:, 0:256], start=True, stop=True)
                last.then_inc(scores_done.sem, 1)

            def turn(l, i):
                pe.wait_ge(probs_ready.sem, probs_ready.at(l, i + 1))
                if i:
                    pe.wait_ge(pt_ready.sem, pt_ready.at(l, i))
                for j in range(2):
                    for k in range(3):
                        last = nc.tensor.transpose(big[:, 2 + j, 128 * k:128 * k + 128],
                                                   S[:, i % 2, j, 128 * k:128 * k + 128], mat[:, IDENT, :])
                last.then_inc(turned.sem, 1)

            def values(l, i):
                pe.wait_ge(pt_ready.sem, pt_ready.at(l, i + 1))
                if i:
                    pe.wait_ge(o_lo.sem, o_lo.at(l, i))
                for j in range(2):
                    for k in range(2):
                        if i < 8:
                            vv = V[:, k, 64 * (2 * i + j):64 * (2 * i + j) + 64]
                        else:
                            vv = SV[:, k, 64 * j:64 * j + 64]
                        dst = po[64 * j:64 * j + 64, 128 * k:256]
                        last = mm(dst, vv, PT[:, i % 2, j, 256 * k:256 + 128 * k], start=(k == 0),
                                  stop=(k == 1))
                last.then_inc(o_done.sem, 1)

            h_op, y_op, z_op = (H_hi, H_lo), (Y_hi, Y_lo), (Z_hi, Z_lo)
            pe.wait_ge(const_in.sem, 80)
            pe.wait_ge(setup.sem, 1)

            with pe.Fori(0, DEPTH) as l:
                mean_x(l, E_N1, 0)
                for u in range(5):
                    pair(l, u, u, h_op, 8, (h_lo, 0) if u == 0 else None)
                for t in (2, 3):
                    pe.wait_ge(*read_out(l, t))
                pe.wait_ge(root_done.sem, root_done.at(l, E_CQ))
                mean(l, E_CQ, 0, [QA[:, 8 + k, :] for k in range(6)], M768, False)
                mean(l, E_CQ, 1, [QA[:, 14 + k, :] for k in range(2)], M256, True)
                pair(l, 5, 5, h_op, 8)
                mean_pair(l, E_KK, T_KK, M64, M32)
                for u in range(6, 9):
                    pair(l, u, u, h_op, 8)
                for g in range(4):
                    pair(l, U_SQ + g, T_SQ + g, h_op, 8)
                    if g:
                        mean_pair(l, E_SQ + g - 1, T_SQ + g - 1, M64, M64)
                pe.wait_ge(lo_ready.sem, lo_ready.at(l, U_SV + 1))
                pe.wait_ge(*read_out(l, T_SV - 2))
                for k in range(2):
                    for c in range(8):
                        tok = slice(128 * k, 128 * k + 128)
                        s, w = U_SV % RING, slice(c * P, c * P + P)
                        dst = acc[:, T_SV % 2, 128 * k:128 * k + 128]
                        mm(dst, H_hi[:, c, tok], whi[:, s, w], start=(c == 0), stop=False)
                        mm(dst, H_hi[:, c, tok], wlo[:, s, w], start=False, stop=False)
                        last = mm(dst, H_lo[:, c, tok], whi[:, s, w], start=False, stop=(c == 7))
                last.then_inc(unit_used.sem, 1)
                mean_pair(l, E_SQ + 3, T_SQ + 3, M64, M64)
                for gate in range(2):
                    u = U_RA + gate
                    pe.wait_ge(lo_ready.sem, lo_ready.at(l, u + 1))
                    for n in range(4):
                        t = T_RA + 4 * gate + n
                        pe.wait_ge(*read_out(l, t - 2))
                        if gate == 0:
                            pe.wait_ge(xc_lo.sem, xc_lo.at(l, n + 1))
                        for m in range(2):
                            for k in range(2):
                                last = product(acc[:, t % 2, 256 * m:256 * m + 256], u % RING,
                                               (n * 4 + m * 2 + k) * P, Z_hi[:, 2 * n + k, :],
                                               Z_lo[:, 2 * n + k, :], k == 0, k == 1)
                        last.then_inc((unit_used if n == 3 else part_done).sem, 1)
                for g in range(4):
                    pair(l, U_LG + g, T_LG + g, h_op, 8)
                for g in range(8):
                    pair(l, U_UQ + g, T_UQ + g, y_op, 6, (lat_lo, 0) if g == 0 else None)
                    if g:
                        mean_pair(l, E_UQ + g - 1, T_UQ + g - 1, MEVEN, MODD)
                pe.wait_ge(lo_ready.sem, lo_ready.at(l, U_UK + 1))
                pe.wait_ge(lat_lo.sem, lat_lo.at(l, 4))
                for g in range(4):
                    t = T_UK + g
                    pe.wait_ge(*read_out(l, t - 2))
                    for h in range(2):
                        for k in range(2):
                            last = product(acc[:, t % 2, 256 * h:256 * h + 256], U_UK % RING,
                                           ((2 * g + h) * 2 + k) * P, Y_hi[:, 6 + k, :], Y_lo[:, 6 + k, :],
                                           k == 0, k == 1)
                    last.then_inc((unit_used if g == 3 else part_done).sem, 1)
                    if g == 0:
                        mean_pair(l, E_UQ + 7, T_UQ + 7, MEVEN, MODD)
                    if g >= 2:
                        mean_pair(l, E_UK + g - 2, T_UK + g - 2, M64, M64)
                pe.wait_ge(lo_ready.sem, lo_ready.at(l, U_UV + 1))
                for g in range(4):
                    t = T_UV + g
                    pe.wait_ge(*read_out(l, t - 2))
                    tok = slice(128 * (g // 2), 128 * (g // 2) + 128)
                    for k in range(2):
                        w = slice(1024 * k + 512 * (g % 2), 1024 * k + 512 * (g % 2) + 512)
                        s, dst = U_UV % RING, acc[:, t % 2, :]
                        mm(dst, Y_hi[:, 6 + k, tok], whi[:, s, w], start=(k == 0), stop=False)
                        mm(dst, Y_hi[:, 6 + k, tok], wlo[:, s, w], start=False, stop=False)
                        last = mm(dst, Y_lo[:, 6 + k, tok], whi[:, s, w], start=False, stop=(k == 1))
                    last.then_inc((unit_used if g == 3 else part_done).sem, 1)
                    if g < 2:
                        mean_pair(l, E_UK + 2 + g, T_UK + 2 + g, M64, M64)
                for s in range(18):
                    if s < 16:
                        scores(l, s)
                    if 1 <= s <= 16:
                        turn(l, s - 1)
                    u, t = U_GB + s, T_GB + s
                    if 4 <= s < 8:
                        pair(l, u, t, z_op, 8, (ob_lo, 0) if s == 4 else None)
                    elif s < 16:
                        pair(l, u, t, h_op, 8)
                    else:
                        if s == 16:
                            pe.wait_ge(o_lo.sem, o_lo.at(l, 8))
                        pair(l, u, t, y_op, 8)
                    if 1 <= s <= 16:
                        values(l, s - 1)
                for u in range(U_BA + 2, U_OUT):
                    if u == U_BC:
                        pe.wait_ge(o_lo.sem, o_lo.at(l, 16))
                    pair(l, u, T_BA + u - U_BA, y_op if u < U_BC else z_op, 8)
                for g in range(4):
                    pair(l, U_OUT + g, T_OUT + g, h_op, 8, (mg_lo, 0) if g == 0 else None)
                mean_x(l, E_N2, 4)

                def up(u, slot, it=0, arrive=False):
                    pe.wait_ge(lo_ready.sem, l * UNITS + it * 6 + (u + 1))
                    for h in range(2):
                        for k in range(8):
                            if arrive and h == 0 and k % 2 == 0:
                                pe.wait_ge(h_lo.sem, h_lo.at(l, 5 + k // 2))
                            last = product(acc[:, slot, 256 * h:256 * h + 256], u % RING, (h * 8 + k) * P,
                                           Y_hi[:, k, :], Y_lo[:, k, :], k == 0, k == 7)
                    last.then_inc(unit_used.sem, 1)

                def down(u, j, slot, it=0, end=False):
                    pe.wait_ge(lo_ready.sem, l * UNITS + it * 6 + (u + 1))
                    pe.wait_ge(f_lo.sem, l * FF_J + it * 3 + (j + 1))
                    for m in range(8):
                        for k in range(2):
                            last = product(big[:, m // 2, 256 * (m % 2):256 * (m % 2) + 256], u % RING,
                                           (k * 8 + m) * P, H_hi[:, 2 * slot + k, :],
                                           H_lo[:, 2 * slot + k, :], False, end and k == 1,
                                           skip_group_check=True)
                    last.then_inc(unit_used.sem, 1)

                pe.wait_ge(h_lo.sem, h_lo.at(l, 5))
                for b in range(4):
                    mm(big[:, b, :], zero[:, :], Y_hi[:, 0:2, :].rearrange("p c t -> p (c t)"), start=True, stop=False, skip_group_check=True)
                up(U_FF, 0, arrive=True)
                with pe.Fori(0, 5) as it:
                    for m in range(3):
                        up(U_FF + 1 + 2 * m, (m + 1) % 3, it)
                        down(U_FF + 2 + 2 * m, m, m, it)
                down(UNITS - 1, 15, 0, end=True)


def kernel(**inputs):
    import numpy as np
    import concourse.bacc as bacc
    from concourse.bass_utils import run_bass_kernel_spmd

    f = {k: np.asarray(v) for k, v in inputs.items()}
    stream, params = pack(f)
    arrays = {"x": np.ascontiguousarray(f["x"][0].T.reshape(DC, P, SEQ).transpose(1, 0, 2)),
              "stream": stream, "params": params, **tables()}
    nc = bacc.Bacc("TRN2", target_bir_lowering=False, num_devices=1, dynamic_dma_scratch_size=1024)
    aps = {k: nc.dram_tensor(f"in_{k}", v.shape, mybir.dt.from_np(v.dtype), kind="ExternalInput").ap()
           for k, v in arrays.items()}
    out = nc.dram_tensor("out_0", (P, DC, SEQ), F32, kind="ExternalOutput").ap()
    trunk(nc, aps["x"], aps["stream"], aps["params"], aps["cs"], aps["mats"], aps["masks"], out)
    r = run_bass_kernel_spmd(nc, [{f"in_{k}": v for k, v in arrays.items()}], core_ids=[0])
    got = r.results[0]["out_0"]
    return np.ascontiguousarray(got.transpose(1, 0, 2).reshape(D, SEQ).T[None])


def tables():
    import numpy as np
    inv = 10000.0 ** (-np.arange(0, ROPE, 2, dtype=np.float32) / ROPE)
    ang = np.arange(SEQ, dtype=np.float32)[None, :] * inv.astype(np.float32)[:, None]
    cos, sin = np.cos(ang).astype(np.float32), np.sin(ang).astype(np.float32)
    c2, s2 = np.concatenate([cos, cos]), np.concatenate([-sin, sin])
    one = np.ones((64, SEQ), np.float32)
    cs = np.stack([np.concatenate([one, c2, s2]), np.concatenate([s2, c2, one]),
                   np.concatenate([s2, c2, c2, s2])], 1)

    def blocks(*sizes):
        m, at = np.zeros((P, P), np.float32), 0
        for n in sizes:
            m[at:at + n, at:at + n] = 1.0 / n
            at += n
        return m
    mats = np.stack([np.eye(P, dtype=np.float32), np.full((P, P), 1 / 1024, np.float32),
                     np.full((P, P), 1 / 768, np.float32), np.full((P, P), 1 / 256, np.float32),
                     blocks(64, 32, 32), blocks(32, 32, 64), blocks(64, 64), blocks(32, 32, 32, 32)], 1)
    q, k = np.arange(P)[:, None], np.arange(P)[None, :]
    causal = np.where(k <= q, 0, NEG).astype(np.float32)
    before = np.where(k > q, 0, NEG).astype(np.float32)
    masks = np.concatenate([causal, before, causal, np.zeros((P, P), np.float32), causal], 1)
    return {"cs": np.ascontiguousarray(cs), "mats": np.ascontiguousarray(mats),
            "masks": np.ascontiguousarray(masks)}


def pack(f):
    import numpy as np

    def stationary(w):
        kc, mc = w.shape[0] // P, w.shape[1] // P
        t = w.reshape(kc, P, mc // 2, 2, P).transpose(2, 1, 3, 0, 4)
        return [u.reshape(P, -1) for u in t]

    swap = np.r_[16:32, 0:16]
    stream = np.zeros((DEPTH * UNITS, P, UNIT), np.float32)
    params = np.zeros((P, DEPTH, NPAR), np.float32)
    for l in range(DEPTH):
        wi = f["w_in"][l]
        cq, ckv, kr, lx, lg, sq, sk, sv, gl = np.split(
            wi, np.cumsum([768, 256, 32, 1024, 1024, 1024, 128, 128]), axis=1)
        krs = kr[:, swap]
        units = stationary(cq) + stationary(ckv)
        units += stationary(np.concatenate([sk, krs, kr, kr, krs], 1))
        units += stationary(lx)
        units += stationary(sq.reshape(D, 2, 8, 64).transpose(0, 2, 1, 3).reshape(D, D))
        units.append(sv.reshape(8, P, P).transpose(1, 0, 2).reshape(P, -1))
        for name in ("w_rg_a", "w_rg_x"):
            w = f[name][l].reshape(4, 2, P, 2, P)
            units.append(w.transpose(2, 0, 3, 1, 4).reshape(P, -1))
        units += stationary(lg)
        uq = f["w_uq"][l].reshape(QRANK, HEADS, 96)
        no, ro = uq[..., :64], uq[..., 64:]
        rs_ = ro[..., swap]
        heads = [np.concatenate([no[:, h], ro[:, h], rs_[:, h]] if h % 2 == 0 else
                                [rs_[:, h], ro[:, h], no[:, h]], 1) for h in range(HEADS)]
        units += stationary(np.concatenate(heads, 1))
        ukv = f["w_ukv"][l].reshape(KVRANK, HEADS, 128)
        uk, uv = ukv[..., :64].reshape(KVRANK, D), ukv[..., 64:].reshape(KVRANK, D)
        units.append(uk.reshape(2, P, 8, P).transpose(1, 2, 0, 3).reshape(P, -1))
        units.append(uv.reshape(2, P, D).transpose(1, 0, 2).reshape(P, -1))
        ga, gb, gc = np.split(gl, 3, axis=1)
        wb = f["w_branch"][l]
        wc = wb[2].reshape(2, 8, 64, D).transpose(1, 0, 2, 3).reshape(D, D)
        units += stationary(gb) + stationary(wb[1]) + stationary(ga) + stationary(gc)
        units += stationary(wb[0]) + stationary(wc) + stationary(f["w_out"][l])
        up = stationary(f["w_ff1"][l])
        down = [w.reshape(2, P, 8, P).transpose(1, 0, 2, 3).reshape(P, -1)
                for w in f["w_ff2"][l].reshape(FF_J, 2 * P, D)]
        units.append(up[0])
        for j in range(FF_J - 1):
            units += [up[j + 1], down[j]]
        units.append(down[-1])
        assert len(units) == UNITS
        for n, u in enumerate(units):
            stream[l * UNITS + n, :, 0:u.shape[1]] = u

        def put(name, v):
            v = np.asarray(v)
            n = dict(PARAM_SIZES)[name]
            params[:, l, PCOL[name]:PCOL[name] + n] = v.reshape(n, P).T

        qn, kn = f["mla_q_norm"][l], f["mla_k_norm"][l]
        put("g1", f["norm1"][l])
        put("g2", f["norm2"][l])
        put("cqg", f["mla_q_a_norm"][l])
        put("ckvg", f["mla_kv_a_norm"][l])
        put("qge", np.concatenate([qn[:64], qn[64:], qn[64:][swap]]))
        put("qgo", np.concatenate([qn[64:][swap], qn[64:], qn[:64]]))
        put("kng", np.tile(kn[:64], 2))
        put("krg", np.concatenate([kn[64:][swap], kn[64:], kn[64:], kn[64:][swap]]))
        put("sqg", np.tile(f["swa_q_norm"][l], 2))
        put("skg", np.tile(f["swa_k_norm"][l], 2))
        for k in range(4):
            put(f"cw{k}", f["conv_w"][l, k])
        put("cb", f["conv_b"][l])
        put("bra", f["b_rg_a"][l])
        put("brx", f["b_rg_x"][l])
        put("lam", f["lru_lambda"][l])
        put("sink", np.repeat(f["swa_sinks"][l], P))
    return stream, params
```
